# Optimizing a Trainium2 kernel written in Bass

```python
import math
import jax, jax.numpy as jnp
from jax import lax
import numpy as np

D_MODEL = 1024
BATCH = 1
SEQ = 1024
DEPTH = 2

HEAD_DIM = 64
Q_HEADS = 8
KV_HEADS = 2
GROUP = Q_HEADS // KV_HEADS
ATTN_WIDTH = Q_HEADS * HEAD_DIM
KV_WIDTH = KV_HEADS * HEAD_DIM
WINDOW = 128
BLOCK = 128
POOL_WIDTH = D_MODEL - ATTN_WIDTH
POOL_WINDOWS = (2, 4, 8, 16)
POOL_GROUPS = len(POOL_WINDOWS)
POOL_GC = POOL_WIDTH // POOL_GROUPS
EVEN_IN = ATTN_WIDTH + 2 * KV_WIDTH + ATTN_WIDTH + POOL_WIDTH + POOL_WIDTH
EVEN_MIX = ATTN_WIDTH + POOL_WIDTH
CONV_WIDTH = D_MODEL
CONV_K = 31
ODD_IN = 3 * CONV_WIDTH
EPS = 1e-6
NEG = -1e30
N_EVEN = (DEPTH + 1) // 2
N_ODD = DEPTH // 2


def rms_norm(x, g):
    xf = x.astype(jnp.float32)
    y = xf * lax.rsqrt(jnp.mean(xf * xf, axis=-1, keepdims=True) + EPS)
    return (y * g.astype(jnp.float32)).astype(x.dtype)

def alibi_slopes(n):
    return jnp.exp2(-8.0 * jnp.arange(1, n + 1, dtype=jnp.float32) / n)

def sliding_window_attention(q, k, v, sinks):
    B, S, _ = q.shape
    nb = S // BLOCK
    q = q.reshape(B, nb, BLOCK, KV_HEADS, GROUP, HEAD_DIM)
    k = k.reshape(B, nb, BLOCK, KV_HEADS, HEAD_DIM)
    v = v.reshape(B, nb, BLOCK, KV_HEADS, HEAD_DIM)
    kpad = jnp.zeros_like(k[:, :1])
    vpad = jnp.zeros_like(v[:, :1])
    kk = jnp.concatenate([jnp.concatenate([kpad, k[:, :-1]], axis=1), k], axis=2)
    vv = jnp.concatenate([jnp.concatenate([vpad, v[:, :-1]], axis=1), v], axis=2)
    scores = jnp.einsum('bnqkgd,bnskd->bnkgqs', q, kk).astype(jnp.float32) * (HEAD_DIM ** -0.5)
    qi = jnp.arange(BLOCK)[:, None] + BLOCK
    sj = jnp.arange(2 * BLOCK)[None, :]
    dist = qi - sj
    key_pos = jnp.arange(nb)[:, None, None] * BLOCK + sj[None] - BLOCK
    valid = (dist >= 0)[None] & (dist < WINDOW)[None] & (key_pos >= 0)
    slopes = alibi_slopes(Q_HEADS).reshape(KV_HEADS, GROUP)
    bias = -slopes[:, :, None, None] * dist.astype(jnp.float32)
    scores = jnp.where(valid[None, :, None, None], scores + bias, NEG)
    sink = sinks.astype(jnp.float32).reshape(KV_HEADS, GROUP)[None, None, :, :, None, None]
    mx = jnp.maximum(jnp.max(scores, axis=-1, keepdims=True), sink)
    p = jnp.exp(scores - mx)
    p = p / (jnp.sum(p, axis=-1, keepdims=True) + jnp.exp(sink - mx))
    out = jnp.einsum('bnkgqs,bnskd->bnqkgd', p.astype(vv.dtype), vv)
    return out.reshape(B, S, ATTN_WIDTH)

def multiscale_pool(u, pool_w, pool_scale):
    B, S, _ = u.shape
    uf = u.astype(jnp.float32).reshape(B, S, POOL_GROUPS, POOL_GC)
    cs = jnp.concatenate([jnp.zeros_like(uf[:, :1]), jnp.cumsum(uf, axis=1)], axis=1)
    t = jnp.arange(S)[:, None]
    win = jnp.array(POOL_WINDOWS, dtype=jnp.int32)[None, :]
    lo = jnp.maximum(t + 1 - win, 0)
    cnt = (t + 1 - lo).astype(jnp.float32)
    lower = cs[:, lo, jnp.arange(POOL_GROUPS)[None, :]]
    pooled = (cs[:, 1:] - lower) / cnt[None, :, :, None] - uf
    y = jnp.einsum('bsgc,gcd->bsgd', pooled, pool_w.astype(jnp.float32))
    y = y * pool_scale.astype(jnp.float32).reshape(POOL_GROUPS, POOL_GC)
    return y.reshape(B, S, POOL_WIDTH).astype(u.dtype)

def even_mixer(h, w_in, sinks, pool_w, pool_scale, w_out):
    proj = h @ w_in
    splits = np.cumsum([ATTN_WIDTH, KV_WIDTH, KV_WIDTH, ATTN_WIDTH, POOL_WIDTH]).tolist()
    q, k, v, ga, u, gb = jnp.split(proj, splits, axis=-1)
    ya = sliding_window_attention(q, k, v, sinks).astype(h.dtype) * jax.nn.silu(ga)
    yb = multiscale_pool(u, pool_w, pool_scale) * jax.nn.silu(gb)
    return jnp.concatenate([ya, yb], axis=-1) @ w_out

def odd_mixer(h, w_in, dw_w, dw_b, ln_g, ln_b, w_out):
    proj = h @ w_in
    a, b, gate = jnp.split(proj, [CONV_WIDTH, 2 * CONV_WIDTH], axis=-1)
    glu = a * jax.nn.sigmoid(b)
    conv = lax.conv_general_dilated(
        glu, dw_w.astype(glu.dtype), window_strides=(1,), padding=[(CONV_K - 1, 0)],
        dimension_numbers=('NWC', 'WIO', 'NWC'), feature_group_count=CONV_WIDTH)
    cf = conv.astype(jnp.float32) + dw_b.astype(jnp.float32)
    mu = jnp.mean(cf, axis=-1, keepdims=True)
    var = jnp.mean(jnp.square(cf - mu), axis=-1, keepdims=True)
    cn = (cf - mu) * lax.rsqrt(var + EPS) * ln_g.astype(jnp.float32) + ln_b.astype(jnp.float32)
    y = jax.nn.silu(cn).astype(h.dtype) * jax.nn.silu(gate)
    return y @ w_out

def first_inputs(seed: int = 0) -> dict:
    key = jax.random.key(seed)
    ks = jax.random.split(key, 16)
    f32 = jnp.float32
    nrm = lambda k, shape, s: jax.random.normal(k, shape, f32) * s
    return {
        'x': nrm(ks[0], (BATCH, SEQ, D_MODEL), 1.0),
        'pre_norm': 1.0 + nrm(ks[1], (DEPTH, D_MODEL), 0.05),
        'post_norm': 1.0 + nrm(ks[2], (DEPTH, D_MODEL), 0.05),
        'a_w_in': nrm(ks[3], (N_EVEN, D_MODEL, EVEN_IN), D_MODEL ** -0.5),
        'a_sinks': nrm(ks[4], (N_EVEN, Q_HEADS), 0.5),
        'b_pool_w': nrm(ks[5], (N_EVEN, POOL_GROUPS, POOL_GC, POOL_GC), POOL_GC ** -0.5),
        'b_pool_scale': 1.0 + nrm(ks[6], (N_EVEN, POOL_WIDTH), 0.1),
        'ab_w_out': nrm(ks[7], (N_EVEN, EVEN_MIX, D_MODEL), EVEN_MIX ** -0.5),
        'c_w_in': nrm(ks[8], (N_ODD, D_MODEL, ODD_IN), D_MODEL ** -0.5),
        'c_dw_w': nrm(ks[9], (N_ODD, CONV_K, 1, CONV_WIDTH), CONV_K ** -0.5),
        'c_dw_b': nrm(ks[10], (N_ODD, CONV_WIDTH), 0.02),
        'c_ln_g': 1.0 + nrm(ks[11], (N_ODD, CONV_WIDTH), 0.05),
        'c_ln_b': nrm(ks[12], (N_ODD, CONV_WIDTH), 0.02),
        'c_w_out': nrm(ks[13], (N_ODD, CONV_WIDTH, D_MODEL), CONV_WIDTH ** -0.5),
    }

def first_block(x, pre_norm, post_norm, a_w_in, a_sinks, b_pool_w, b_pool_scale, ab_w_out,
              c_w_in, c_dw_w, c_dw_b, c_ln_g, c_ln_b, c_w_out):
    for layer in range(DEPTH):
        h = rms_norm(x, pre_norm[layer])
        if layer % 2 == 0:
            i = layer // 2
            y = even_mixer(h, a_w_in[i], a_sinks[i], b_pool_w[i], b_pool_scale[i], ab_w_out[i])
        else:
            i = layer // 2
            y = odd_mixer(h, c_w_in[i], c_dw_w[i], c_dw_b[i], c_ln_g[i], c_ln_b[i], c_w_out[i])
        x = x + rms_norm(y, post_norm[layer])
    return x


DEPTH_2 = 1

N_META = 16
D_MIX = D_MODEL
D_ATTN = D_MIX // 2
N_ATTN_HEADS = D_ATTN // HEAD_DIM
D_CONV = D_MIX - D_ATTN
N_CONV_GROUPS = D_CONV // HEAD_DIM
CONV_WIDTH_2 = 3
D_FF = 4 * D_MODEL
Q_BLOCK = 128
EPS_2 = 1e-5
NEG_INF = -1e30
D_IN_PROJ = 3 * D_ATTN + N_ATTN_HEADS + 3 * D_CONV


def rms_norm_2(x, g):
    xf = x.astype(jnp.float32)
    y = xf * lax.rsqrt(jnp.mean(xf * xf, axis=-1, keepdims=True) + EPS_2)
    return (y * g.astype(jnp.float32)).astype(x.dtype)

def head_rms_norm(y, n_groups, g):
    b, l, c = y.shape
    yf = y.astype(jnp.float32).reshape(b, l, n_groups, c // n_groups)
    yf = yf * lax.rsqrt(jnp.mean(yf * yf, axis=-1, keepdims=True) + EPS_2)
    return (yf.reshape(b, l, c) * g.astype(jnp.float32)).astype(y.dtype)

def forgetting_attention(q, k, v, log_f):
    L = q.shape[1]
    cum = jnp.cumsum(log_f.astype(jnp.float32), axis=1).transpose(0, 2, 1)
    scale = HEAD_DIM ** -0.5
    n_blocks = (L - N_META) // Q_BLOCK
    bounds = [(0, N_META)] + [(N_META + i * Q_BLOCK, N_META + (i + 1) * Q_BLOCK)
                              for i in range(n_blocks)]
    outs = []
    for lo, hi in bounds:
        qb, kb, vb = q[:, lo:hi], k[:, :hi], v[:, :hi]
        s = jnp.einsum('bqhd,bkhd->bhqk', qb, kb,
                       preferred_element_type=jnp.float32) * scale
        decay = cum[:, :, lo:hi, None] - cum[:, :, None, :hi]
        causal = jnp.arange(hi)[None, :] <= jnp.arange(lo, hi)[:, None]
        s = jnp.where(causal, s + decay, NEG_INF)
        p = jax.nn.softmax(s, axis=-1)
        outs.append(jnp.einsum('bhqk,bkhd->bqhd', p.astype(vb.dtype), vb))
    return jnp.concatenate(outs, axis=1)

def causal_depthwise_conv(u, w):
    L = u.shape[1]
    up = jnp.pad(u, ((0, 0), (CONV_WIDTH_2 - 1, 0), (0, 0)))
    y = w[0] * up[:, 0:L]
    for kk in range(1, CONV_WIDTH_2):
        y = y + w[kk] * up[:, kk:kk + L]
    return y

def second_inputs(seed: int = 0) -> dict:
    key = jax.random.key(seed)
    ks = jax.random.split(key, 14)
    f32 = jnp.float32
    x = jax.random.normal(ks[0], (BATCH, SEQ, D_MODEL), f32)
    meta_tokens = jax.random.normal(ks[1], (N_META, D_MODEL), f32)
    norm_mix_g = 1.0 + 0.02 * jax.random.normal(ks[2], (DEPTH_2, D_MODEL), f32)
    w_in = jax.random.normal(ks[3], (DEPTH_2, D_MODEL, D_IN_PROJ), f32) * D_MODEL ** -0.5
    b_f = (jnp.linspace(1.0, 6.0, N_ATTN_HEADS, dtype=f32)[None, :]
           + 0.1 * jax.random.normal(ks[4], (DEPTH_2, N_ATTN_HEADS), f32))
    conv_w = jax.random.normal(ks[5], (DEPTH_2, CONV_WIDTH_2, D_CONV), f32) * CONV_WIDTH_2 ** -0.5
    out_norm_g = 1.0 + 0.02 * jax.random.normal(ks[6], (DEPTH_2, D_MIX), f32)
    w_out = jax.random.normal(ks[7], (DEPTH_2, D_MIX, D_MODEL), f32) * D_MIX ** -0.5
    norm_mlp_g = 1.0 + 0.02 * jax.random.normal(ks[8], (DEPTH_2, D_MODEL), f32)
    w_ff1 = jax.random.normal(ks[9], (DEPTH_2, D_MODEL, D_FF), f32) * D_MODEL ** -0.5
    w_ff2 = jax.random.normal(ks[10], (DEPTH_2, D_FF, D_MODEL), f32) * D_FF ** -0.5
    final_norm_g = 1.0 + 0.02 * jax.random.normal(ks[11], (D_MODEL,), f32)
    return {"x": x, "meta_tokens": meta_tokens, "norm_mix_g": norm_mix_g, "w_in": w_in,
            "b_f": b_f, "conv_w": conv_w, "out_norm_g": out_norm_g, "w_out": w_out,
            "norm_mlp_g": norm_mlp_g, "w_ff1": w_ff1, "w_ff2": w_ff2,
            "final_norm_g": final_norm_g}

def second_block(x, meta_tokens, norm_mix_g, w_in, b_f, conv_w, out_norm_g, w_out,
              norm_mlp_g, w_ff1, w_ff2, final_norm_g):
    B = x.shape[0]
    meta = jnp.broadcast_to(meta_tokens.astype(x.dtype)[None], (B, N_META, D_MODEL))
    h = jnp.concatenate([meta, x], axis=1)
    L = h.shape[1]
    split_at = [D_ATTN, 2 * D_ATTN, 3 * D_ATTN, 3 * D_ATTN + N_ATTN_HEADS,
                3 * D_ATTN + N_ATTN_HEADS + D_CONV, 3 * D_ATTN + N_ATTN_HEADS + 2 * D_CONV]
    for layer in range(DEPTH_2):
        xn = rms_norm_2(h, norm_mix_g[layer])
        proj = jnp.einsum('bld,de->ble', xn, w_in[layer])
        q, k, v, f_logit, b_gate, c_gate, u = jnp.split(proj, split_at, axis=-1)
        log_f = jax.nn.log_sigmoid(f_logit.astype(jnp.float32) + b_f[layer].astype(jnp.float32))
        hs = (B, L, N_ATTN_HEADS, HEAD_DIM)
        y_attn = forgetting_attention(q.reshape(hs), k.reshape(hs), v.reshape(hs), log_f)
        y_attn = y_attn.reshape(B, L, D_ATTN)
        y_conv = b_gate * causal_depthwise_conv(c_gate * u, conv_w[layer].astype(u.dtype))
        y = jnp.concatenate([head_rms_norm(y_attn, N_ATTN_HEADS, out_norm_g[layer, :D_ATTN]),
                             head_rms_norm(y_conv, N_CONV_GROUPS, out_norm_g[layer, D_ATTN:])],
                            axis=-1)
        h = h + jnp.einsum('ble,ed->bld', y, w_out[layer])
        hn = rms_norm_2(h, norm_mlp_g[layer])
        a = jnp.square(jax.nn.relu(jnp.einsum('bld,df->blf', hn, w_ff1[layer])))
        h = h + jnp.einsum('blf,fd->bld', a, w_ff2[layer])
    h = rms_norm_2(h, final_norm_g)
    return h[:, N_META:]


def setup_inputs(seed=0):
    out = dict(first_inputs(seed))
    for name, value in second_inputs(seed + 1).items():
        if name != "x":
            out[name + "_2"] = value
    return out


def reference(
    x, pre_norm, post_norm, a_w_in, a_sinks, b_pool_w, b_pool_scale, ab_w_out, c_w_in, c_dw_w,
    c_dw_b, c_ln_g, c_ln_b, c_w_out, meta_tokens_2, norm_mix_g_2, w_in_2, b_f_2, conv_w_2,
    out_norm_g_2, w_out_2, norm_mlp_g_2, w_ff1_2, w_ff2_2, final_norm_g_2,
):
    x = first_block(
        x, pre_norm, post_norm, a_w_in, a_sinks, b_pool_w, b_pool_scale, ab_w_out, c_w_in,
        c_dw_w, c_dw_b, c_ln_g, c_ln_b, c_w_out,
    )
    return second_block(
        x, meta_tokens_2, norm_mix_g_2, w_in_2, b_f_2, conv_w_2, out_norm_g_2, w_out_2,
        norm_mlp_g_2, w_ff1_2, w_ff2_2, final_norm_g_2,
    )


_drawn_inputs = setup_inputs


def setup_inputs(seed=0):
    import zlib

    import numpy as np

    out = dict(_drawn_inputs(seed))
    spreads = {}
    factors = {'a_sinks': 3.003,
     'c_ln_b': 3.596,
     'norm_mix_g_2': 3.249,
     'out_norm_g_2': 40.784,
     'norm_mlp_g_2': 12.432,
     'final_norm_g_2': 19.163}
    for name, (base, spread) in spreads.items():
        noise = np.random.default_rng([zlib.crc32(name.encode()), seed]).standard_normal(out[name].shape)
        drawn = base * np.exp(spread * noise) if base else spread * noise
        out[name] = __import__('jax').numpy.asarray(drawn.astype(out[name].dtype))
    for name, factor in factors.items():
        out[name] = (out[name] * factor).astype(out[name].dtype)
    return out
```

```python
from contextlib import ExitStack

import concourse.bass as bass
from concourse import mybir

ALU = mybir.AluOpType
ACT = mybir.ActivationFunctionType
AX = mybir.AxisListType
F32 = mybir.dt.float32
F32R = mybir.dt.float32r
BF16 = mybir.dt.bfloat16
I32 = mybir.dt.int32

P = 128
S = 1024
D = 1024
KD = D // P
NB = S // P
HALF = 512
HD = 64
HEADS = 8
GROUP = 4
META = 16
L = META + S
DF = 4 * D
TAPS = 31
NEG = -1e30
WINDOWS = (2, 4, 8, 16)
EPS_A, EPS_B = 1e-6, 1e-5
QK_SCALE = HD ** -0.5

C_IN0 = 0
C_OUT0 = C_IN0 + 18
C_IN1 = C_OUT0 + KD
C_OUT1 = C_IN1 + 3 * KD
C_IN2 = C_OUT1 + KD
C_OUT2 = C_IN2 + 25
C_MLP = C_OUT2 + KD
FG = 4
NG = DF // (FG * P)
C_END = C_MLP + 2 * NG * FG
Q0, K0, V0, U0, GB0, GA0 = 0, 4, 5, 6, 10, 14
USE0 = KD
USE_MLP = USE0 + C_MLP
SP_IN0, SP_OUT0, SP_IN1, SP_OUT1, SP_IN2, SP_OUT2, SP_MLP = range(7)
G_PRE0, G_POST0, G_PRE1, G_POST1, G_DWB, G_LNG, G_LNB, G_MIX, G_OUTN, G_MLP = range(10)
NGAIN = 10
N_PRE0, N_POST0, N_PRE1, N_LN, N_POST1, N_MIX, N_MLP = range(7)
NORM_EPS = (EPS_A, EPS_A, EPS_A, EPS_A, EPS_A, EPS_B, EPS_B)


class Signal:

    def __init__(self, sem):
        self.sem = sem
        self.n = 0

    def by(self, ins):
        self.n += 1
        ins.then_inc(self.sem, 1)
        return self.n


def pieces(lo, hi):
    while lo < hi:
        end = min(hi, (lo // HALF + 1) * HALF)
        yield lo, end
        lo = end


def build(nc, x, meta, weights, gains, taps, pool_w, pool_scale, conv_w, b_f, sinks, final_g, out):
    with ExitStack() as ctx:
        top = [-(-nc.sbuf_base // 64) * 64]

        def fixed(name, shape, dt=F32):
            t = nc.alloc_sbuf_tensor_at(name, shape, dt, offset=top[0])
            size = 2 if dt == BF16 else 4
            for n in shape[1:]:
                size *= n
            top[0] += -(-size // 32) * 32
            return t

        def at(name, shape, offset, dt=F32):
            return nc.alloc_sbuf_tensor_at(name, shape, dt, offset=offset)

        X = fixed("X", [P, KD, S])
        o_xh = top[0]
        XH = fixed("XH", [P, KD, S], F32R)
        o_xl = top[0]
        XL = fixed("XL", [P, KD, S], F32R)
        WRAW = fixed("WRAW", [P, 2, D])
        WH = fixed("WH", [P, 2, D], F32R)
        WL = fixed("WL", [P, 2, D], F32R)
        RB = fixed("RB", [P, S])
        IDENT = fixed("IDENT", [P, P])
        GROUPS = fixed("GROUPS", [P, P])
        IDENTB = fixed("IDENTB", [P, P], BF16)
        MASKB = fixed("MASKB", [P, P], BF16)
        COLSEL = fixed("COLSEL", [P, 15])
        ROWSEL = fixed("ROWSEL", [8, 8, P])
        GAINS = fixed("GAINS", [P, NGAIN, KD])
        PSCALE = fixed("PSCALE", [P, 4])
        CONVW = fixed("CONVW", [P, 4, 3])
        BF = fixed("BF", [8, 1])
        SINKS = fixed("SINKS", [P, HEADS])
        EPS = fixed("EPS", [P, 2])
        o_dist = top[0]
        DIST = fixed("DIST", [P, 2 * P])
        XMH = at("XMH", [P, KD, META], o_dist, F32R)
        XML = at("XML", [P, KD, META], o_dist + 512, F32R)
        INVC = fixed("INVC", [P, 16])
        RT = fixed("RT", [8, P])
        RR = fixed("RR", [8, P])
        SMALL = fixed("SMALL", [P, 96])
        area = top[0]
        assert area + 76416 + 256 <= nc.sbuf_usable_end, (area, nc.sbuf_usable_end)

        XTOK = at("XTOK", [P, NB, D], area)
        Y = at("Y", [P, KD, S], area)
        SQ = at("SQ", [P, 2, S], area + 61440)
        SSUM = at("SSUM", [P, S], area + 61440 + 8192)
        P0 = at("P0", [P, 18, S], area)
        PAD = [at(f"PAD{n}", [P, 16 + S], area + 65024 + 4160 * n) for n in range(2)]
        PW = at("PW", [P, 4, P], area + 73728)
        VT0 = at("VT0", [P, NB, P], o_xh)
        BIAS = at("BIAS", [P, HEADS, 2 * P], o_xh + 4096)
        YT0 = at("YT0", [P, 2, GROUP * HD], o_xh + 12288)
        SS0 = at("SS0", [P, 2, GROUP, 2 * P], o_xl)
        PT0 = at("PT0", [P, 2 * GROUP, P], o_xl + 8192)
        G1 = at("G1", [P, KD, TAPS - 1 + S], area)
        GATE = at("GATE", [P, KD, S], area + 33728)
        T1 = [at(f"T1_{n}", [P, S], area + 66496 + 4096 * n) for n in range(2)]
        TAPW = at("TAPW", [P, KD, TAPS], area + 74688)
        ONES = at("ONES", [P, P], area + 75680)
        SQ1 = at("SQ1", [P, 2, S], o_xl + 16384)
        SSUM1 = at("SSUM1", [P, S], o_xl + 24576)
        MU = at("MU", [P, S], o_xl + 28672)
        K2 = at("K2", [P, 4, L], area)
        CU = at("CU", [P, 4, L], area + 16640)
        VF = at("VF", [P, 4, L], area + 33280)
        Q2 = at("Q2", [P, 4, S], area + 33280)
        VT2 = at("VT2", [P, NB + 1, 4 * P], area + 49920)
        T2 = [at(f"T2_{n}", [P, L], area + 68352 + 4160 * n) for n in range(2)]
        XMT = at("XMT", [META, D], area + 40960)
        XMS = at("XMS", [META, D], area + 45056)
        NEGC = at("NEGC", [P, HEADS, L], o_xh)
        SS2 = [at(f"SS2_{n}", [P, L], o_xh + 33280 + 4160 * n) for n in range(2)]
        PT2 = at("PT2", [P, 2, 4 * P], o_xh + 41600)
        YT2 = at("YT2", [P, NB, HEADS * HD], o_xh + 45696)
        YSQ = at("YSQ", [P, HEADS * HD], o_xh + 62080)
        AH = at("AH", [P, 2, FG, S], area, F32R)
        AL = at("AL", [P, 2, FG, S], area + 32768, F32R)
        TM = at("TM", [P, 2, S], area + 65536)
        GFIN = at("GFIN", [P, D], o_xh)
        OT = at("OT", [P, 2, D], o_xh + 4096)
        OSQ = at("OSQ", [P, D], o_xh + 12288)

        PS = ctx.enter_context(nc.psum_tensor("PS", [P, 8 * HALF], F32))

        def slot(n):
            return PS[:, (n % 2) * S:(n % 2 + 1) * S]

        def bank(b, n=1):
            return PS[:, b * HALF:(b + n) * HALF]

        def sem(name):
            return ctx.enter_context(nc.semaphore(name))

        x_in = [sem(f"x_in{b}") for b in range(NB)]
        small_in = sem("small_in")
        taps_in = sem("taps_in")
        meta_in = sem("meta_in")
        gfin_in = sem("gfin_in")
        w_in = [sem("w_in0"), sem("w_in1")]
        w_hi = sem("w_hi")
        w_ready = sem("w_ready")
        consts = sem("consts")
        psum_full = sem("psum_full")
        evacuated = sem("evacuated")
        x_hi = sem("x_hi")
        x_split = sem("x_split")
        squared = sem("squared")
        sq_added = sem("sq_added")
        n_sum = sem("n_sum")
        n_root = sem("n_root")
        n_inv = sem("n_inv")
        n_wide = sem("n_wide")
        n_rb = sem("n_rb")
        step = Signal(sem("vector_step"))
        astep = Signal(sem("scalar_step"))
        x_new = sem("x_new")
        gate_done = sem("gate_done")
        pooled = sem("pooled")
        pool_out = sem("pool_out")
        pool_taken = sem("pool_taken")
        v0_turned = sem("v0_turned")
        v0_ready = sem("v0_ready")
        s0_ready = sem("s0_ready")
        s0_max = sem("s0_max")
        p0_ready = sem("p0_ready")
        pt0_ready = sem("pt0_ready")
        pt0_copied = sem("pt0_copied")
        o0_ready = sem("o0_ready")
        yt0_ready = sem("yt0_ready")
        ya_turned = sem("ya_turned")
        ya_ready = sem("ya_ready")
        b_sig = sem("b_sig")
        cf_ready = sem("cf_ready")
        mu_sum = sem("mu_sum")
        cf_mid = sem("cf_mid")
        cn_ready = sem("cn_ready")
        cn_silu = sem("cn_silu")
        y1_ready = sem("y1_ready")
        m_scaled = sem("m_scaled")
        m_turned = sem("m_turned")
        m_root = sem("m_root")
        m_hi = sem("m_hi")
        m_split = sem("m_split")
        f_in = sem("f_in")
        f_log = sem("f_log")
        cum_ready = sem("cum_ready")
        v2_turned = sem("v2_turned")
        v2_taken = sem("v2_taken")
        nc_wide = sem("nc_wide")
        nc_ready = sem("nc_ready")
        s2_ready = sem("s2_ready")
        s2_max = sem("s2_max")
        p2_ready = sem("p2_ready")
        pt2_ready = sem("pt2_ready")
        pt2_copied = sem("pt2_copied")
        o2_ready = sem("o2_ready")
        o2_taken = sem("o2_taken")
        ysum_ready = sem("ysum_ready")
        yroot = sem("yroot")
        ynorm = sem("ynorm")
        y2_turned = sem("y2_turned")
        y2_ready = sem("y2_ready")
        yc_sq = sem("yc_sq")
        yc_sum = sem("yc_sum")
        yc_root = sem("yc_root")
        step_b = Signal(sem("conv2_ready"))
        yc_ready = sem("yc_ready")
        a_sq = sem("a_sq")
        a_hi = sem("a_hi")
        a_split = sem("a_split")
        o_turned = sem("o_turned")
        o_root = sem("o_root")
        o_ready = sem("o_ready")
        stored = [sem("stored0"), sem("stored1")]

        block = ctx.enter_context(nc.Block())

        I_C, I_B, I_F, I_V, I_K, I_Q = 0, 8, 12, 13, 17, 21
        UNITS0 = 2 * NB
        UNITS2 = HEADS * NB
        ngroups = [-(-(i + 2) // 4) for i in range(NB)]

        def tiles2(i):
            hi = META + P * (i + 1)
            return [(P * j, min(P, hi - P * j)) for j in range(i + 2)]

        @block.sync
        def _(sp):
            for b in range(NB):
                sp.dma_start(XTOK[:, b, :], x[b * P:(b + 1) * P, :]).then_inc(x_in[b], 16)
            sp.dma_start(WRAW[:, 0, :], weights[0]).then_inc(w_in[0], 16)
            sp.dma_start(WRAW[:, 1, :], weights[1]).then_inc(w_in[1], 16)
            with sp.Fori(1, C_END // 2) as i:
                for u in range(2):
                    sp.wait_ge(w_ready, i * 2 + (u - 1))
                    sp.dma_start(WRAW[:, u, :], weights[i * 2 + u]).then_inc(w_in[u], 16)
            sp.wait_ge(w_ready, C_END - 1)
            sp.dma_start(WRAW[:, 0, :], weights[C_END - 1]).then_inc(w_in[0], 16)
            sp.wait_ge(psum_full, USE_MLP + 4 + 12 * (NG - 1))
            sp.dma_start(GFIN[:], final_g).then_inc(gfin_in, 16)
            for b in range(NB):
                sp.wait_ge(o_ready, b + 1)
                sp.dma_start(out[b * P:(b + 1) * P, :], OT[:, b % 2, :]).then_inc(stored[b % 2], 16)
            for n in range(2):
                sp.wait_ge(stored[n], 16 * (NB // 2))

        @block.gpsimd
        def _(pool):
            made = Signal(consts)

            def const(ins):
                pool.wait_ge(made.sem, made.by(ins))

            g = nc.gpsimd
            const(g.memset(IDENT[:], 0.0))
            const(g.affine_select(out=IDENT[:], in_=IDENT[:], compare_op=ALU.not_equal, fill=1.0, base=0,
                                  pattern=[[-1, P]], channel_multiplier=1))
            const(g.memset(COLSEL[:], 0.0))
            const(g.memset(COLSEL[:, 7:8], 1.0))
            const(g.memset(ROWSEL[:], 0.0))
            const(g.affine_select(out=ROWSEL[:], in_=ROWSEL[:], compare_op=ALU.not_equal, fill=1.0, base=0,
                                  pattern=[[-1, 8], [0, P]], channel_multiplier=1))
            const(g.memset(EPS[:, 0:1], EPS_A))
            const(g.memset(EPS[:, 1:2], EPS_B))
            const(g.memset(GROUPS[:], 0.0))
            const(g.memset(GROUPS[0:HD, 0:HD], 1.0))
            const(g.memset(GROUPS[HD:P, HD:P], 1.0))
            const(g.tensor_copy(IDENTB[:], IDENT[:]))
            const(g.memset(MASKB[:], 0.0))
            const(g.affine_select(out=MASKB[:], in_=MASKB[:], compare_op=ALU.is_ge, fill=NEG, base=0,
                                  pattern=[[-1, P]], channel_multiplier=1))
            for t in range(16):
                const(g.memset(INVC[:, t:t + 1], 1.0 / (t + 1)))
            const(g.iota(DIST[:], pattern=[[8, 2 * P]], base=-8 * P, channel_multiplier=-8,
                         allow_small_or_imprecise_dtypes=True))
            const(g.affine_select(out=DIST[:], in_=DIST[:], compare_op=ALU.is_ge, fill=NEG, base=P,
                                  pattern=[[-1, 2 * P]], channel_multiplier=1))
            const(g.affine_select(out=DIST[:], in_=DIST[:], compare_op=ALU.is_ge, fill=NEG, base=-1,
                                  pattern=[[1, 2 * P]], channel_multiplier=-1))

            def split(c, u):
                g.tensor_tensor(WH[:, u, :], WRAW[:, u, :], COLSEL[:, 7:8].to_broadcast([P, D]),
                                ALU.mult).then_inc(w_hi, 1)
                pool.wait_ge(w_hi, c + 1)
                g.tensor_tensor(WL[:, u, :], WRAW[:, u, :], WH[:, u, :].bitcast(F32), ALU.subtract)\
                    .then_inc(w_ready, 1)

            for u in range(2):
                pool.wait_ge(w_in[u], 16)
                split(u, u)
            assert C_MLP % 2 == 1
            with pool.Fori(1, C_MLP // 2) as i:
                for u in range(2):
                    pool.wait_ge(w_in[u], i * 16 + 16)
                    pool.wait_ge(psum_full, i * 2 + (u - 2 + USE0 + 1))
                    split(i * 2 + u, u)

            def mlp_split(c, u, full, i):
                pool.wait_ge(w_in[u], i * (16 * 8) + 16 * (c // 2 + 1))
                pool.wait_ge(psum_full, i * 24 + full)
                split(i * 16 + c, u)

            order = ["A"] * FG
            for n in range(NG - 1):
                order += ["A"] * FG + ["B"] * FG
            order += ["B"] * FG
            done = [USE_MLP - 1, USE_MLP]
            for kind in order:
                done.append(done[-1] + (1 if kind == "A" else 2))
            body = 4 * FG
            last = len(order) - FG - 3 * body
            c = C_MLP - 1
            pool.wait_ge(w_in[c % 2], 16 * (c // 2 + 1))
            pool.wait_ge(psum_full, USE_MLP - 2)
            split(c, c % 2)
            for j in range(FG):
                c = C_MLP + j
                pool.wait_ge(w_in[c % 2], 16 * (c // 2 + 1))
                pool.wait_ge(psum_full, done[j])
                split(c, c % 2)
            with pool.Fori(0, 3) as i:
                for j in range(FG, FG + body):
                    c = C_MLP + j
                    mlp_split(c, c % 2, done[j], i)
            for j in range(FG + 3 * body, len(order)):
                c = C_MLP + j
                pool.wait_ge(w_in[c % 2], 16 * (c // 2 + 1))
                pool.wait_ge(psum_full, done[j])
                split(c, c % 2)
            assert last == 2 * FG + FG

        @block.tensor
        def _(pe):
            full = Signal(psum_full)

            def transposes_in():
                pe.wait_ge(consts, 2)
                for k in range(KD):
                    if k >= 2:
                        pe.wait_ge(evacuated, k - 1)
                    for b in range(NB):
                        if k == 0:
                            pe.wait_ge(x_in[b], 16)
                        last = nc.tensor.transpose(slot(k)[:, b * P:(b + 1) * P],
                                                   XTOK[:, b, k * P:(k + 1) * P], IDENT[:])
                    full.by(last)

            def three(dst, wh, wl, xh, xl, first, last, cols=None):
                for n, (w, v) in enumerate(((wh, xh), (wh, xl), (wl, xh))):
                    for a, b in cols or ((0, HALF), (HALF, S)):
                        m = nc.tensor.matmul(dst[:, a:b], w, v[:, a:b], start=first and n == 0,
                                             stop=last and n == 2)
                return m

            def chunk(c, i, sp, meta_dst=None):
                u = c % 2
                use = USE0 + c
                n = 0 if i is None else i * 2
                pe.wait_ge(w_ready, n + (c + 1))
                pe.wait_ge(evacuated, n + (use - 1))
                for k in range(KD):
                    pe.wait_ge(x_split, KD * sp + k + 1)
                    w = (WH[:, u, k * P:(k + 1) * P], WL[:, u, k * P:(k + 1) * P])
                    if meta_dst is not None:
                        three(meta_dst, *w, XMH[:, k, :], XML[:, k, :], k == 0, k == KD - 1, ((0, META),))
                    m = three(slot(use), *w, XH[:, k, :], XL[:, k, :], k == 0, k == KD - 1)
                m.then_inc(psum_full, 1)

            def dense(c, n, sp, meta=False, norm_n=None):
                def one(c, i):
                    chunk(c, i, sp, bank(4 + c % 2)[:, 0:META] if meta else None)

                if norm_n is not None:
                    one(c, None)
                    one(c + 1, None)
                    norm(norm_n)
                    c, n = c + 2, n - 2
                with pe.Fori(0, n // 2) as i:
                    for u in range(2):
                        one(c + u, i)

            def norm(n):
                src = SSUM1 if n == N_LN else SSUM
                pe.wait_ge(consts, 6)
                pe.wait_ge(sq_added, (KD - 1) * (n + 1))
                for b in range(NB):
                    m = nc.tensor.matmul(bank(4)[0:8, P:2 * P], COLSEL[:, 7 - b:15 - b], src[:, b * P:(b + 1) * P],
                                         start=b == 0, stop=b == NB - 1)
                m.then_inc(n_sum, 1)
                pe.wait_ge(n_inv, n + 1)
                for b in range(NB):
                    m = nc.tensor.matmul(bank(6, 2)[:, b * P:(b + 1) * P], ROWSEL[:, b, :], RR[:],
                                         start=True, stop=True)
                m.then_inc(n_wide, 1)

            def block0():
                pe.wait_ge(evacuated, USE0 + V0 + 1)
                for b in range(NB):
                    m = nc.tensor.transpose(bank(6, 2)[:, b * P:(b + 1) * P], P0[:, V0, b * P:(b + 1) * P], IDENT[:])
                m.then_inc(v0_turned, 1)
                pe.wait_ge(evacuated, USE0 + C_OUT0)
                pe.wait_ge(small_in, 16 * 6)
                for g in range(4):
                    pe.wait_ge(pooled, g + 1)
                    if g >= 2:
                        pe.wait_ge(pool_taken, g - 1)
                    for h in range(2):
                        m = nc.tensor.matmul(slot(g)[:, h * HALF:(h + 1) * HALF], PW[:, g, :],
                                             P0[:, U0 + g, h * HALF:(h + 1) * HALF], start=True, stop=True)
                    m.then_inc(pool_out, 1)
                pe.wait_ge(pool_taken, 4)
                pe.wait_ge(v0_ready, 1)

                def scores(t):
                    n, half = divmod(t, 2)
                    r = half * HD
                    if t >= 2:
                        pe.wait_ge(s0_max, t - 1)
                    k0 = P if n == 0 else 0
                    for j in range(GROUP):
                        m = nc.tensor.matmul(slot(t)[:, j * 2 * P + k0:(j + 1) * 2 * P],
                                             P0[r:r + HD, Q0 + j, n * P:(n + 1) * P],
                                             P0[r:r + HD, K0, (n - 1) * P + k0:(n + 1) * P],
                                             start=True, stop=True)
                    m.then_inc(s0_ready, 1)

                def keys_down(t):
                    pe.wait_ge(p0_ready, t + 1)
                    if t >= 1:
                        pe.wait_ge(pt0_copied, t)
                    first = 1 if t < 2 else 0
                    for j in range(GROUP):
                        for h in range(first, 2):
                            m = nc.tensor.transpose(bank(4, 2)[:, (2 * j + h) * P:(2 * j + h + 1) * P],
                                                    SS0[:, t % 2, j, h * P:(h + 1) * P], IDENT[:])
                    m.then_inc(pt0_ready, 1)

                def values(t):
                    n, half = divmod(t, 2)
                    first = 1 if n == 0 else 0
                    pe.wait_ge(pt0_copied, t + 1)
                    if t >= 1:
                        pe.wait_ge(yt0_ready, t)
                    for j in range(GROUP):
                        for h in range(first, 2):
                            m = nc.tensor.matmul(bank(6)[:, j * HD:(j + 1) * HD], PT0[:, 2 * j + h, :],
                                                 VT0[:, n - 1 + h, half * HD:(half + 1) * HD],
                                                 start=h == first, stop=h == 1)
                    m.then_inc(o0_ready, 1)

                def turn(t):
                    pe.wait_ge(yt0_ready, t + 1)
                    if t >= 1:
                        pe.wait_ge(ya_ready, t)
                    for m_ in range(2):
                        m = nc.tensor.transpose(bank(7)[:, m_ * P:(m_ + 1) * P], YT0[:, t % 2, m_ * P:(m_ + 1) * P],
                                                IDENT[:])
                    m.then_inc(ya_turned, 1)

                scores(0)
                scores(1)
                for t in range(UNITS0):
                    keys_down(t)
                    if t + 2 < UNITS0:
                        scores(t + 2)
                    values(t)
                    if t >= 1:
                        turn(t - 1)
                turn(UNITS0 - 1)

            def mean1():
                for c in range(KD):
                    pe.wait_ge(cf_ready, c + 1)
                    for h in range(2):
                        m = nc.tensor.matmul(bank(4 + h), ONES[:], G1[:, c, TAPS - 1 + h * HALF:TAPS - 1 + (h + 1) * HALF],
                                             start=c == 0, stop=c == KD - 1, skip_group_check=True)
                m.then_inc(mu_sum, 1)

            def meta_in2():
                pe.wait_ge(m_scaled, 1)
                for k in range(KD):
                    m = nc.tensor.transpose(bank(5)[:, k * META:(k + 1) * META], XMS[:, k * P:(k + 1) * P],
                                            IDENT[0:META, 0:META])
                m.then_inc(m_turned, 1)

            def v2_turn():
                for c in range(4):
                    for g in range(3):
                        n = 3 * c + g
                        b = 6 + n % 2
                        if n >= 2:
                            pe.wait_ge(v2_taken, n - 1)
                        if n == 0:
                            pe.wait_ge(evacuated, USE0 + C_IN2 + I_K)
                            pe.wait_ge(yc_root, 4)
                        for j in range(4 * g, min(4 * g + 4, NB + 1)):
                            w = min(P, L - j * P)
                            m = nc.tensor.transpose(bank(b)[0:w, (j % 4) * P:(j % 4 + 1) * P],
                                                    VF[:, c, j * P:j * P + w], IDENT[:])
                        m.then_inc(v2_turned, 1)

            def attention2():
                pe.wait_ge(cum_ready, 1)
                pe.wait_ge(evacuated, USE0 + C_OUT2)

                def wide(h):
                    if h >= 2:
                        pe.wait_ge(nc_ready, h - 1)
                    for a, b in pieces(0, L):
                        m = nc.tensor.matmul(PS[:, (h % 2) * 3 * HALF + a:(h % 2) * 3 * HALF + b], ROWSEL[:, h, :],
                                             T2[0][0:8, a:b], start=True, stop=True)
                    m.then_inc(nc_wide, 1)

                for h in range(HEADS):
                    wide(h)
                pe.wait_ge(nc_ready, HEADS)
                pe.wait_ge(v2_taken, 12)

                def scores(t):
                    i, h = divmod(t, HEADS)
                    r, base = (h % 2) * HD, (t % 2) * 3 * HALF
                    hi = META + P * (i + 1)
                    if t >= 2:
                        pe.wait_ge(s2_max, t - 1)
                        if i == NB - 1:
                            pe.wait_ge(o2_taken, t - 1)
                    diag = list(pieces(hi - P, hi))
                    for a, b in pieces(0, hi):
                        masks = [(x, y) for x, y in diag if a <= x < b]
                        m = nc.tensor.matmul(PS[:, base + a:base + b], Q2[r:r + HD, h // 2, i * P:(i + 1) * P],
                                             K2[r:r + HD, h // 2, a:b], start=True, stop=True)
                        for x, y in masks:
                            m = nc.tensor.matmul(PS[:, base + x:base + y], IDENTB[:],
                                                 MASKB[:, x - (hi - P):y - (hi - P)], start=False, stop=True,
                                                 skip_group_check=True)
                    m.then_inc(s2_ready, 1)

                groups = [0]

                def values(t, ahead=None):
                    i, h = divmod(t, HEADS)
                    base = (t % 2) * 3 * HALF + 2 * HALF + HD
                    pe.wait_ge(p2_ready, t + 1)
                    tl = tiles2(i)
                    gs = [tl[a:a + 4] for a in range(0, len(tl), 4)]

                    def turn(g):
                        n = groups[0] + g
                        if n >= 2:
                            pe.wait_ge(pt2_copied, n - 1)
                        for j, (k, w) in enumerate(gs[g]):
                            m = nc.tensor.transpose(bank(6 + n % 2)[0:w, j * P:(j + 1) * P], SS2[t % 2][:, k:k + w],
                                                    IDENT[:])
                        m.then_inc(pt2_ready, 1)

                    def weigh(g):
                        n = groups[0] + g
                        pe.wait_ge(pt2_copied, n + 1)
                        for j, (k, w) in enumerate(gs[g]):
                            m = nc.tensor.matmul(PS[:, base:base + HD], PT2[0:w, n % 2, j * P:(j + 1) * P],
                                                 VT2[0:w, k // P, h * HD:(h + 1) * HD], start=k == 0,
                                                 stop=k == tl[-1][0], skip_group_check=True)
                        return m

                    for g in range(min(2, len(gs))):
                        turn(g)
                    if ahead is not None:
                        scores(ahead)
                    for g in range(len(gs)):
                        m = weigh(g)
                        if g + 2 < len(gs):
                            turn(g + 2)
                    m.then_inc(o2_ready, 1)
                    groups[0] += len(gs)

                scores(0)
                scores(1)
                for t in range(UNITS2):
                    if t + 2 < UNITS2 - HEADS:
                        values(t, t + 2)
                    else:
                        values(t)
                        if t + 2 < UNITS2:
                            scores(t + 2)

            def heads_conv(c):
                pe.wait_ge(yc_sq, c + 1)
                if c >= 1:
                    pe.wait_ge(yc_root, c)
                for h in range(2):
                    m = nc.tensor.matmul(bank(6 + h), GROUPS[:], K2[:, c, h * HALF:(h + 1) * HALF],
                                         start=True, stop=True)
                m.then_inc(yc_sum, 1)

            def heads_turn():
                for c in range(4):
                    if c >= 2:
                        pe.wait_ge(y2_ready, c - 1)
                    for i in range(NB):
                        pe.wait_ge(ynorm, i + 1)
                        m = nc.tensor.transpose(slot(c)[:, i * P:(i + 1) * P], YT2[:, i, c * P:(c + 1) * P], IDENT[:])
                    m.then_inc(y2_turned, 1)

            def mlp():
                def first_kind(c, use, g, i=None):
                    for j in range(FG):
                        if g == 0 and j == 2:
                            norm(N_MLP)
                        n_w, n_u = (0, 0) if i is None else (i * 16, i * 24)
                        cc, uu = c + j, use + j
                        pe.wait_ge(w_ready, n_w + (cc + 1))
                        pe.wait_ge(evacuated, n_u + (uu - 1))
                        for k in range(KD):
                            pe.wait_ge(x_split, KD * SP_MLP + k + 1)
                            m = three(slot(uu), WH[:, cc % 2, k * P:(k + 1) * P], WL[:, cc % 2, k * P:(k + 1) * P],
                                      XH[:, k, :], XL[:, k, :], k == 0, k == KD - 1)
                        m.then_inc(psum_full, 1)

                def second_kind(c, use, g, i=None):
                    gp = g % 2
                    for j in range(FG):
                        n_w, n_u, n_g = (0, 0, 0) if i is None else (i * 16, i * 24, i * (2 * FG))
                        cc = c + j
                        pe.wait_ge(w_ready, n_w + (cc + 1))
                        for e in range(2):
                            uu = use + 2 * j + e
                            pe.wait_ge(evacuated, n_u + (uu - 1))
                            for k in range(FG):
                                pe.wait_ge(a_split, n_g + (FG * g + k + 1))
                                w0 = (e * FG + k) * P
                                m = three(slot(uu), WH[:, cc % 2, w0:w0 + P], WL[:, cc % 2, w0:w0 + P],
                                          AH[:, gp, k, :], AL[:, gp, k, :], k == 0, k == FG - 1)
                            m.then_inc(psum_full, 1)

                c, use = C_MLP, USE_MLP
                first_kind(c, use, 0)
                c, use = c + FG, use + FG
                with pe.Fori(0, 3) as i:
                    for g in range(2):
                        first_kind(c + 2 * FG * g, use + 3 * FG * g, g + 1, i)
                        second_kind(c + 2 * FG * g + FG, use + 3 * FG * g + FG, g, i)
                c, use = c + 3 * 4 * FG, use + 3 * 6 * FG
                first_kind(c, use, NG - 1)
                second_kind(c + FG, use + FG, NG - 2)
                second_kind(c + 2 * FG, use + 3 * FG, NG - 1)
                return use + 5 * FG

            def turn_out(use):
                for b in range(NB):
                    pe.wait_ge(evacuated, use)
                    if b >= 2:
                        pe.wait_ge(o_ready, b - 1)
                    for k in range(KD):
                        m = nc.tensor.transpose(slot(use + b)[:, k * P:(k + 1) * P], X[:, k, b * P:(b + 1) * P], IDENT[:])
                    m.then_inc(o_turned, 1)

            transposes_in()
            dense(C_IN0, 18, SP_IN0, norm_n=N_PRE0)
            block0()
            dense(C_OUT0, KD, SP_OUT0)
            norm(N_POST0)
            dense(C_IN1, 3 * KD, SP_IN1, norm_n=N_PRE1)
            mean1()
            norm(N_LN)
            dense(C_OUT1, KD, SP_OUT1)
            norm(N_POST1)
            meta_in2()
            pe.wait_ge(m_split, 1)
            dense(C_IN2 + I_C, 8, SP_IN2, meta=True, norm_n=N_MIX)
            dense(C_IN2 + I_B, 4, SP_IN2)
            heads_conv(0)
            chunk(C_IN2 + I_F, None, SP_IN2, bank(4 + I_F % 2)[:, 0:META])
            heads_conv(1)
            dense(C_IN2 + I_V, 2, SP_IN2, meta=True)
            heads_conv(2)
            dense(C_IN2 + I_V + 2, 2, SP_IN2, meta=True)
            heads_conv(3)
            dense(C_IN2 + I_K, 4, SP_IN2, meta=True)
            v2_turn()
            dense(C_IN2 + I_Q, 4, SP_IN2)
            attention2()
            heads_turn()
            dense(C_OUT2, KD, SP_OUT2)
            turn_out(mlp())

        @block.scalar
        def _(act):
            for t, src in ((GAINS, gains), (PSCALE, pool_scale), (CONVW, conv_w), (BF, b_f),
                           (SINKS, sinks), (PW, pool_w)):
                act.dma_start(t[:], src).then_inc(small_in, 16)
            act.wait_ge(consts, 8)
            act.wait_ge(small_in, 16 * 6)

            def hi(sp, k, src, gain=None):
                scale = 1.0 if gain is None else GAINS[:, gain, k:k + 1]
                nc.scalar.activation(XH[:, k, :], src, ACT.Copy, scale=scale).then_inc(x_hi, 1)

            def square(n, k, src, sq=SQ):
                if k == 0 and n > 0:
                    act.wait_ge(sq_added, (KD - 1) * n)
                if k >= 2:
                    act.wait_ge(sq_added, (KD - 1) * n + max(1, k - 2))
                nc.scalar.activation(sq[:, k % 2, :], src, ACT.Square).then_inc(squared, 1)

            def norm(n):
                act.wait_ge(n_sum, n + 1)
                nc.scalar.activation(RT[:], bank(4)[0:8, P:2 * P], ACT.Sqrt, scale=1.0 / D,
                                     bias=EPS[0:8, 0:1] if NORM_EPS[n] == EPS_A else EPS[0:8, 1:2]).then_inc(n_root, 1)

            for k in range(KD):
                act.wait_ge(evacuated, k + 1)
                hi(SP_IN0, k, X[:, k, :], G_PRE0)
            for k in range(KD):
                square(N_PRE0, k, X[:, k, :])
            norm(N_PRE0)
            for c in range(8):
                act.wait_ge(evacuated, USE0 + GB0 + c + 1)
                g = P0[:, GB0 + c, :]
                nc.scalar.activation(g, g, ACT.Silu).then_inc(gate_done, 1)
            for t in range(UNITS0 + 1):
                if t < UNITS0:
                    act.wait_ge(s0_max, t + 1)
                    k0 = P if t < 2 else 0
                    for j in range(GROUP):
                        s = SS0[:, t % 2, j, k0:2 * P]
                        nc.scalar.activation(s, s, ACT.Exp, bias=SMALL[:, 8 * (t % 2) + j:8 * (t % 2) + j + 1],
                                             accum_out=SMALL[:, 16 + 4 * (t % 4) + j:17 + 4 * (t % 4) + j])
                    sk = SMALL[:, 32 + 4 * (t % 4):36 + 4 * (t % 4)]
                    nc.scalar.activation(sk, sk, ACT.Exp).then_inc(p0_ready, 1)
                if t >= 1:
                    act.wait_ge(pt0_ready, t)
                    if t >= 2:
                        act.wait_ge(o0_ready, t - 1)
                    if t <= 2:
                        for j in range(GROUP):
                            ins = nc.scalar.copy(PT0[:, 2 * j + 1, :], bank(4, 2)[:, (2 * j + 1) * P:(2 * j + 2) * P])
                    else:
                        ins = nc.scalar.copy(PT0[:].rearrange("p a b -> p (a b)"), bank(4, 2))
                    ins.then_inc(pt0_copied, 1)
            for k in range(KD):
                if k == 0:
                    act.wait_ge(ya_ready, UNITS0)
                    act.dma_start(TAPW[:], taps).then_inc(taps_in, 16)
                hi(SP_OUT0, k, P0[:, GA0 + k if k < 4 else GB0 + k - 4, :])

            def post(c, n_norm, sp, gain, between=None):
                for k in range(KD):
                    act.wait_ge(evacuated, USE0 + c + k + 1)
                    square(n_norm, k, Y[:, k, :])
                norm(n_norm)
                if between is not None:
                    between()
                for k in range(KD):
                    act.wait_ge(x_new, KD * (n_norm == N_POST1) + k + 1)
                    hi(sp, k, X[:, k, :], gain)
                for k in range(KD):
                    square(n_norm + 1, k, X[:, k, :])
                norm(n_norm + 1)

            post(C_OUT0, N_POST0, SP_IN1, G_PRE1)
            for c in range(KD):
                act.wait_ge(evacuated, USE0 + C_IN1 + 3 * c + 2)
                nc.scalar.activation(T1[0][:], T1[0][:], ACT.Sigmoid).then_inc(b_sig, 1)
                act.wait_ge(evacuated, USE0 + C_IN1 + 3 * c + 3)
                nc.scalar.activation(GATE[:, c, :], GATE[:, c, :], ACT.Silu).then_inc(gate_done, 1)
            for k in range(KD):
                act.wait_ge(cf_mid, k + 1)
                square(N_LN, k, G1[:, k, TAPS - 1:], SQ1)
            norm(N_LN)
            for k in range(KD):
                act.wait_ge(cn_ready, k + 1)
                g = G1[:, k, TAPS - 1:]
                nc.scalar.activation(g, g, ACT.Silu, bias=GAINS[:, G_LNB, k:k + 1]).then_inc(cn_silu, 1)
                if k >= 1:
                    act.wait_ge(y1_ready, k)
                    hi(SP_OUT1, k - 1, G1[:, k - 1, TAPS - 1:])
            act.wait_ge(y1_ready, KD)
            hi(SP_OUT1, KD - 1, G1[:, KD - 1, TAPS - 1:])
            act.wait_ge(evacuated, USE0 + C_OUT1 + 1)
            act.dma_start(XMT[:], meta).then_inc(meta_in, 16)

            def meta_rms():
                act.wait_ge(meta_in, 16)
                act.wait_ge(astep.sem, astep.by(nc.scalar.activation(XMS[:], XMT[:], ACT.Square,
                                                                    accum_out=SMALL[0:META, 72:73])))
                nc.scalar.activation(SMALL[0:META, 73:74], SMALL[0:META, 72:73], ACT.Sqrt, scale=1.0 / D,
                                     bias=EPS[0:META, 1:2]).then_inc(m_root, 1)
                act.wait_ge(m_turned, 1)
                for k in range(KD):
                    ins = nc.scalar.activation(XMH[:, k, :], bank(5)[:, k * META:(k + 1) * META], ACT.Copy,
                                               scale=GAINS[:, G_MIX, k:k + 1])
                ins.then_inc(m_hi, 1)

            post(C_OUT1, N_POST1, SP_IN2, G_MIX, meta_rms)
            for c in range(4):
                if c == 0:
                    act.wait_ge(step_b.sem, 4)
                nc.scalar.activation(K2[:, c, 0:S], CU[:, c, META:], ACT.Square).then_inc(yc_sq, 1)
            for c in range(4):
                act.wait_ge(yc_sum, c + 1)
                nc.scalar.activation(K2[:, c, 0:S], bank(6, 2), ACT.Sqrt, scale=1.0 / HD,
                                     bias=EPS[:, 1:2]).then_inc(yc_root, 1)
                if c == 1:
                    act.wait_ge(f_in, 1)
                    z, e = T2[0][0:8, :], T2[1][0:8, :]
                    for f, s, b in ((ACT.Abs, 1.0, 0.0), (ACT.Exp, -1.0, 0.0), (ACT.Ln, 1.0, 1.0)):
                        ins = nc.scalar.activation(e, z if f == ACT.Abs else e, f, scale=s, bias=b)
                        if f == ACT.Ln:
                            ins.then_inc(f_log, 1)
                        else:
                            act.wait_ge(astep.sem, astep.by(ins))
            copied = 0
            for t in range(UNITS2 + 1):
                if t < UNITS2:
                    i = t // HEADS
                    hi_ = META + P * (i + 1)
                    act.wait_ge(s2_max, t + 1)
                    s = SS2[t % 2][:, 0:hi_]
                    nc.scalar.activation(s, s, ACT.Exp, bias=SMALL[:, 2 + t % 2:3 + t % 2],
                                         accum_out=SMALL[:, 76 + t % 4:77 + t % 4]).then_inc(p2_ready, 1)
                if t >= 1:
                    tl = tiles2((t - 1) // HEADS)
                    for a in range(0, len(tl), 4):
                        grp = tl[a:a + 4]
                        act.wait_ge(pt2_ready, copied + 1)
                        w = sum(1 for _, n in grp if n == P)
                        if w:
                            ins = nc.scalar.copy(PT2[:, copied % 2, 0:w * P], bank(6 + copied % 2)[:, 0:w * P])
                        if w < len(grp):
                            ins = nc.scalar.copy(PT2[0:META, copied % 2, w * P:(w + 1) * P],
                                                 bank(6 + copied % 2)[0:META, w * P:(w + 1) * P])
                        ins.then_inc(pt2_copied, 1)
                        copied += 1
            act.wait_ge(ysum_ready, NB)
            nc.scalar.activation(SMALL[:, 8:72], SMALL[:, 8:72], ACT.Sqrt, scale=1.0 / HD,
                                 bias=EPS[:, 1:2]).then_inc(yroot, 1)
            for k in range(KD):
                act.wait_ge(y2_ready, 4)
                hi(SP_OUT2, k, Q2[:, k, :] if k < 4 else CU[:, k - 4, META:], G_OUTN)
            act.wait_ge(evacuated, USE_MLP)
            for k in range(KD):
                hi(SP_MLP, k, X[:, k, :], G_MLP)
            for k in range(KD):
                square(N_MLP, k, X[:, k, :])
            norm(N_MLP)
            def hidden(g, use, i=None):
                for j in range(FG):
                    n_c, n_u = (0, 0) if i is None else (i * (2 * FG), i * 24)
                    act.wait_ge(evacuated, n_u + (use + j + 1))
                    nc.scalar.activation(TM[:, j % 2, :], TM[:, j % 2, :], ACT.Square).then_inc(a_sq, 1)
                    act.wait_ge(a_sq, n_c + (FG * g + j + 1))
                    nc.scalar.activation(AH[:, g % 2, j, :], TM[:, j % 2, :], ACT.Copy).then_inc(a_hi, 1)

            hidden(0, USE_MLP)
            with act.Fori(0, 3) as i:
                hidden(1, USE_MLP + FG, i)
                hidden(2, USE_MLP + 4 * FG, i)
            hidden(NG - 1, USE_MLP + FG + 3 * FG * (NG - 2))
            for b in range(NB):
                act.wait_ge(o_turned, b + 1)
                if b >= 2:
                    act.wait_ge(o_ready, b - 1)
                r = SMALL[:, 76 + b % 2:77 + b % 2]
                ins = nc.scalar.activation(OSQ[:], slot(USE_MLP + 3 * NG * FG + b), ACT.Square, accum_out=r)
                act.wait_ge(astep.sem, astep.by(ins))
                nc.scalar.activation(SMALL[:, 78 + b % 2:79 + b % 2], r, ACT.Sqrt, scale=1.0 / D,
                                     bias=EPS[:, 1:2]).then_inc(o_root, 1)

        v = nc.vector

        @block.vector
        def _(dve):
            def then(ins):
                dve.wait_ge(step.sem, step.by(ins))

            def lo(sp, k, src, gain=None):
                dve.wait_ge(x_hi, KD * sp + k + 1)
                h = XH[:, k, :].bitcast(F32)
                if gain is None:
                    ins = v.tensor_tensor(XL[:, k, :], src, h, ALU.subtract)
                else:
                    ins = v.scalar_tensor_tensor(out=XL[:, k, :], in0=src, scalar=GAINS[:, gain, k:k + 1], in1=h,
                                                 op0=ALU.mult, op1=ALU.subtract)
                ins.then_inc(x_split, 1)

            def add_square(n, k, sq=SQ, ssum=SSUM):
                if k == 0:
                    return
                dve.wait_ge(squared, KD * n + k + 1)
                if k >= 2:
                    dve.wait_ge(sq_added, (KD - 1) * n + k - 1)
                v.tensor_tensor(ssum[:], sq[:, 0, :] if k == 1 else ssum[:], sq[:, k % 2, :],
                                ALU.add).then_inc(sq_added, 1)

            def norm(n):
                dve.wait_ge(n_root, n + 1)
                v.reciprocal(RR[:], RT[:]).then_inc(n_inv, 1)
                dve.wait_ge(n_wide, n + 1)
                v.tensor_copy(RB[:], bank(6, 2)).then_inc(n_rb, 1)
                dve.wait_ge(n_rb, n + 1)

            def take(c, dst, op=None):
                use = USE0 + c
                dve.wait_ge(psum_full, use + 1)
                if op is None:
                    v.tensor_tensor(dst, slot(use), RB[:], ALU.mult).then_inc(evacuated, 1)
                else:
                    v.tensor_copy(dst, slot(use)).then_inc(evacuated, 1)
                dve.wait_ge(evacuated, use + 1)

            for k in range(KD):
                dve.wait_ge(psum_full, k + 1)
                v.tensor_copy(X[:, k, :], slot(k)).then_inc(evacuated, 1)
                if k >= 1:
                    lo(SP_IN0, k - 1, X[:, k - 1, :], G_PRE0)
            lo(SP_IN0, KD - 1, X[:, KD - 1, :], G_PRE0)
            for k in range(KD):
                add_square(N_PRE0, k)
            norm(N_PRE0)
            with dve.Fori(0, U0 // 2 + 2) as i:
                for u in range(2):
                    use = USE0 + u
                    dve.wait_ge(psum_full, i * 2 + (use + 1))
                    v.tensor_tensor(P0[:, i * 2 + u, :], slot(use), RB[:], ALU.mult).then_inc(evacuated, 1)
            then(v.memset(PAD[0][:, 0:16], 0.0))
            then(v.memset(PAD[1][:, 0:16], 0.0))

            def windows(g):
                u = P0[:, U0 + g, :]
                then(v.tensor_copy(PAD[0][:, 16:], u))
                a = 0
                for lvl in range(g + 1):
                    sh = 1 << lvl
                    then(v.tensor_tensor(PAD[1 - a][:, 16:], PAD[a][:, 16:], PAD[a][:, 16 - sh:16 + S - sh], ALU.add))
                    a = 1 - a
                w = WINDOWS[g]
                then(v.tensor_tensor(PAD[a][:, 16:16 + w], PAD[a][:, 16:16 + w], INVC[:, 0:w], ALU.mult))
                then(v.tensor_tensor(P0[:, U0 + g, 0:w], PAD[a][:, 16:16 + w], P0[:, U0 + g, 0:w], ALU.subtract))
                v.scalar_tensor_tensor(out=P0[:, U0 + g, w:], in0=PAD[a][:, 16 + w:], scalar=1.0 / w,
                                       in1=P0[:, U0 + g, w:], op0=ALU.mult, op1=ALU.subtract).then_inc(pooled, 1)
                dve.wait_ge(pooled, g + 1)

            dve.wait_ge(evacuated, USE0 + GB0)
            dve.wait_ge(consts, 33)
            for c in range(4):
                windows(c)
                dve.wait_ge(psum_full, USE0 + GB0 + c + 1)
                v.tensor_tensor(P0[:, GB0 + c, :], slot(USE0 + GB0 + c), RB[:], ALU.mult).then_inc(evacuated, 1)
            for c in range(4):
                dve.wait_ge(psum_full, USE0 + GA0 + c + 1)
                v.tensor_tensor(P0[:, GA0 + c, :], slot(USE0 + GA0 + c), RB[:], ALU.mult).then_inc(evacuated, 1)
            dve.wait_ge(v0_turned, 1)
            v.tensor_copy(VT0[:].rearrange("p a b -> p (a b)"), bank(6, 2)).then_inc(v0_ready, 1)
            for h in range(HEADS):
                then(v.tensor_scalar(BIAS[:, h, :], DIST[:], 2.0 ** -(h + 1), None, ALU.mult))
            for g in range(4):
                dve.wait_ge(pool_out, g + 1)
                dve.wait_ge(gate_done, g + 1)
                gb = P0[:, GB0 + g, :]
                v.scalar_tensor_tensor(out=gb, in0=slot(g), scalar=PSCALE[:, g:g + 1], in1=gb, op0=ALU.mult,
                                       op1=ALU.mult).then_inc(pool_taken, 1)
            dve.wait_ge(pool_taken, 4)
            dve.wait_ge(gate_done, 8)

            def maxima0(t):
                n, half = divmod(t, 2)
                dve.wait_ge(s0_ready, t + 1)
                if t >= 2:
                    dve.wait_ge(pt0_ready, t - 1)
                if t >= 1:
                    dve.wait_ge(s0_max, t)
                k0 = P if n == 0 else 0
                mx = SMALL[:, 48:52]
                for j in range(GROUP):
                    ins = v.tensor_tensor_reduce(SS0[:, t % 2, j, k0:], slot(t)[:, j * 2 * P + k0:(j + 1) * 2 * P],
                                                 BIAS[:, half * GROUP + j, k0:], QK_SCALE, -3e38, ALU.add, ALU.max,
                                                 SMALL[:, 48 + j:49 + j])
                then(ins)
                sinks_ = SINKS[:, half * GROUP:(half + 1) * GROUP]
                then(v.tensor_tensor(mx, mx, sinks_, ALU.max))
                then(v.tensor_scalar(SMALL[:, 8 * (t % 2):8 * (t % 2) + 4], mx, -1.0, None, ALU.mult))
                v.tensor_tensor(SMALL[:, 32 + 4 * (t % 4):36 + 4 * (t % 4)], sinks_, mx,
                                ALU.subtract).then_inc(s0_max, 1)

            def output0(t):
                n, half = divmod(t, 2)
                dve.wait_ge(p0_ready, t + 1)
                if t >= 1:
                    dve.wait_ge(yt0_ready, t)
                den = SMALL[:, 52:56]
                then(v.tensor_tensor(den, SMALL[:, 16 + 4 * (t % 4):20 + 4 * (t % 4)],
                                     SMALL[:, 32 + 4 * (t % 4):36 + 4 * (t % 4)], ALU.add))
                then(v.reciprocal(SMALL[:, 56:60], den))
                dve.wait_ge(o0_ready, t + 1)
                if t >= 2:
                    dve.wait_ge(ya_turned, t - 1)
                for j in range(GROUP):
                    ins = v.tensor_scalar(YT0[:, t % 2, j * HD:(j + 1) * HD], bank(6)[:, j * HD:(j + 1) * HD],
                                          SMALL[:, 56 + j:57 + j], None, ALU.mult)
                ins.then_inc(yt0_ready, 1)

            def gate0(t):
                n, half = divmod(t, 2)
                dve.wait_ge(ya_turned, t + 1)
                ga = P0[:, GA0 + 2 * half:GA0 + 2 * half + 2, n * P:(n + 1) * P]
                v.tensor_tensor(ga, bank(7)[:, 0:2 * P].rearrange("p (a b) -> p a b", a=2), ga,
                                ALU.mult).then_inc(ya_ready, 1)

            maxima0(0)
            maxima0(1)
            for t in range(UNITS0):
                if t + 2 < UNITS0:
                    maxima0(t + 2)
                output0(t)
                if t >= 1:
                    gate0(t - 1)
            gate0(UNITS0 - 1)
            for k in range(KD):
                lo(SP_OUT0, k, P0[:, GA0 + k if k < 4 else GB0 + k - 4, :])

            def post(c, n_norm, gain_post, sp, gain, between=None):
                for k in range(KD):
                    use = USE0 + c + k
                    dve.wait_ge(psum_full, use + 1)
                    v.tensor_copy(Y[:, k, :], slot(use)).then_inc(evacuated, 1)
                    if k >= 1:
                        add_square(n_norm, k - 1)
                add_square(n_norm, KD - 1)
                norm(n_norm)
                if between is not None:
                    between()
                for k in range(KD):
                    then(v.scalar_tensor_tensor(out=Y[:, k, :], in0=Y[:, k, :], scalar=GAINS[:, gain_post, k:k + 1],
                                                in1=RB[:], op0=ALU.mult, op1=ALU.mult))
                    v.tensor_tensor(X[:, k, :], X[:, k, :], Y[:, k, :], ALU.add).then_inc(x_new, 1)
                    if k >= 1:
                        lo(sp, k - 1, X[:, k - 1, :], gain)
                lo(sp, KD - 1, X[:, KD - 1, :], gain)
                for k in range(KD):
                    add_square(n_norm + 1, k)
                norm(n_norm + 1)

            post(C_OUT0, N_POST0, G_POST0, SP_IN1, G_PRE1)

            then(v.memset(G1[:, :, 0:TAPS - 1], 0.0))
            then(v.memset(ONES[:], 1.0))
            dve.wait_ge(taps_in, 16)

            def conv(c, first, end):
                acc = T1[1][:]
                for j in range(first, end):
                    src, tap = G1[:, c, j:j + S], TAPW[:, c, j:j + 1]
                    if j == 0:
                        then(v.tensor_scalar(acc, src, tap, GAINS[:, G_DWB, c:c + 1], ALU.mult, ALU.add))
                    elif j < TAPS - 1:
                        then(v.scalar_tensor_tensor(out=acc, in0=src, scalar=tap, in1=acc, op0=ALU.mult, op1=ALU.add))
                    else:
                        v.scalar_tensor_tensor(out=src, in0=src, scalar=tap, in1=acc, op0=ALU.mult,
                                               op1=ALU.add).then_inc(cf_ready, 1)
                        dve.wait_ge(cf_ready, c + 1)

            for c in range(KD):
                w = C_IN1 + 3 * c
                take(w, G1[:, c, TAPS - 1:])
                if c >= 1:
                    conv(c - 1, 0, TAPS // 3)
                take(w + 1, T1[0][:])
                if c >= 1:
                    conv(c - 1, TAPS // 3, 2 * TAPS // 3)
                dve.wait_ge(b_sig, c + 1)
                then(v.tensor_tensor(G1[:, c, TAPS - 1:], G1[:, c, TAPS - 1:], T1[0][:], ALU.mult))
                take(w + 2, GATE[:, c, :])
                if c >= 1:
                    conv(c - 1, 2 * TAPS // 3, TAPS)
            conv(KD - 1, 0, TAPS)
            dve.wait_ge(cf_ready, KD)
            dve.wait_ge(mu_sum, 1)
            then(v.tensor_scalar(MU[:], bank(4, 2), 1.0 / D, None, ALU.mult))
            for k in range(KD):
                g = G1[:, k, TAPS - 1:]
                v.tensor_tensor(g, g, MU[:], ALU.subtract).then_inc(cf_mid, 1)
                if k >= 1:
                    add_square(N_LN, k - 1, SQ1, SSUM1)
            add_square(N_LN, KD - 1, SQ1, SSUM1)
            norm(N_LN)
            dve.wait_ge(gate_done, 16)
            for k in range(KD + 2):
                if k < KD:
                    g = G1[:, k, TAPS - 1:]
                    if k == 0:
                        dve.wait_ge(cf_mid, KD)
                    v.scalar_tensor_tensor(out=g, in0=g, scalar=GAINS[:, G_LNG, k:k + 1], in1=RB[:], op0=ALU.mult,
                                           op1=ALU.mult).then_inc(cn_ready, 1)
                if 1 <= k <= KD:
                    dve.wait_ge(cn_silu, k)
                    g = G1[:, k - 1, TAPS - 1:]
                    v.tensor_tensor(g, g, GATE[:, k - 1, :], ALU.mult).then_inc(y1_ready, 1)
                if k >= 2:
                    dve.wait_ge(y1_ready, k - 1)
                    lo(SP_OUT1, k - 2, G1[:, k - 2, TAPS - 1:])

            def meta_operand():
                dve.wait_ge(m_root, 1)
                r = SMALL[0:META, 74:75]
                then(v.reciprocal(r, SMALL[0:META, 73:74]))
                v.tensor_scalar(XMS[:], XMT[:], r, None, ALU.mult).then_inc(m_scaled, 1)
                dve.wait_ge(m_hi, 1)
                for k in range(KD):
                    ins = v.scalar_tensor_tensor(out=XML[:, k, :], in0=bank(5)[:, k * META:(k + 1) * META],
                                                 scalar=GAINS[:, G_MIX, k:k + 1], in1=XMH[:, k, :].bitcast(F32),
                                                 op0=ALU.mult, op1=ALU.subtract)
                ins.then_inc(m_split, 1)

            post(C_OUT1, N_POST1, G_POST1, SP_IN2, G_MIX, meta_operand)

            def take_meta(c, dst, factor=None, rows=P):
                src = bank(4 + c % 2)[0:rows, 0:META]
                dve.wait_ge(psum_full, USE0 + c + 1)
                if factor is None:
                    then(v.tensor_copy(dst, src))
                else:
                    then(v.tensor_tensor(dst, src, factor, ALU.mult))

            for c in range(4):
                w = C_IN2 + I_C + 2 * c
                take_meta(w, T2[0][:, 0:META])
                take(w, T2[0][:, META:])
                take_meta(w + 1, CU[:, c, 0:META], T2[0][:, 0:META])
                take(w + 1, CU[:, c, META:])
                then(v.tensor_tensor(CU[:, c, META:], CU[:, c, META:], T2[0][:, META:], ALU.mult))
            for c in range(4):
                t, b = T2[0][:, 0:S], T2[1][:, 0:S]
                then(v.tensor_scalar(t, CU[:, c, META - 2:L - 2], CONVW[:, c, 0:1], None, ALU.mult))
                for j in (1, 2):
                    then(v.scalar_tensor_tensor(out=t, in0=CU[:, c, META - 2 + j:L - 2 + j], scalar=CONVW[:, c, j:j + 1],
                                                in1=t, op0=ALU.mult, op1=ALU.add))
                take(C_IN2 + I_B + c, b)
                dve.wait_ge(step_b.sem, step_b.by(v.tensor_tensor(CU[:, c, META:], t, b, ALU.mult)))
            w = C_IN2 + I_F
            take_meta(w, T2[0][0:8, 0:META], rows=8)
            dve.wait_ge(psum_full, USE0 + w + 1)
            v.tensor_tensor(T2[0][0:8, META:], slot(USE0 + w)[0:8, :], RB[0:8, :], ALU.mult).then_inc(evacuated, 1)
            dve.wait_ge(evacuated, USE0 + w + 1)
            v.tensor_scalar(T2[0][0:8, :], T2[0][0:8, :], BF[:], None, ALU.add).then_inc(f_in, 1)

            def heads_conv(c):
                dve.wait_ge(yc_root, c + 1)
                then(v.reciprocal(K2[:, c, 0:S], K2[:, c, 0:S]))
                then(v.tensor_tensor(CU[:, c, META:], CU[:, c, META:], K2[:, c, 0:S], ALU.mult))

            heads_conv(0)
            dve.wait_ge(f_log, 1)
            z, e = T2[0][0:8, :], T2[1][0:8, :]
            then(v.scalar_tensor_tensor(out=z, in0=z, scalar=0.0, in1=e, op0=ALU.min, op1=ALU.subtract))
            then(v.tensor_tensor_scan(e, z, z, 0.0, ALU.add, ALU.min))
            v.tensor_scalar(z, e, -1.0 / QK_SCALE, None, ALU.mult).then_inc(cum_ready, 1)
            for c in range(4):
                w = C_IN2 + I_V + c
                take_meta(w, VF[:, c, 0:META])
                take(w, VF[:, c, META:])
                if c < 3:
                    heads_conv(c + 1)
            for c in range(4):
                w = C_IN2 + I_K + c
                take_meta(w, K2[:, c, 0:META])
                take(w, K2[:, c, META:])
            for n in range(12):
                c, g = divmod(n, 3)
                dve.wait_ge(v2_turned, n + 1)
                if g < 2:
                    v.tensor_copy(VT2[:, 4 * g:4 * g + 4, c * P:(c + 1) * P],
                                  bank(6 + n % 2).rearrange("p (a b) -> p a b", a=4)).then_inc(v2_taken, 1)
                else:
                    v.tensor_copy(VT2[0:META, NB, c * P:(c + 1) * P],
                                  bank(6 + n % 2)[0:META, 0:P]).then_inc(v2_taken, 1)
            for c in range(4):
                take(C_IN2 + I_Q + c, Q2[:, c, :])
            for h in range(HEADS):
                dve.wait_ge(nc_wide, h + 1)
                v.tensor_copy(NEGC[:, h, :], PS[:, (h % 2) * 3 * HALF:(h % 2) * 3 * HALF + L]).then_inc(nc_ready, 1)
            dve.wait_ge(nc_ready, HEADS)

            def maxima2(t):
                i, h = divmod(t, HEADS)
                hi_, base = META + P * (i + 1), (t % 2) * 3 * HALF
                dve.wait_ge(s2_ready, t + 1)
                if t >= 1:
                    dve.wait_ge(s2_max, t)
                then(v.tensor_tensor_reduce(SS2[t % 2][:, 0:hi_], PS[:, base:base + hi_], NEGC[:, h, 0:hi_], QK_SCALE,
                                            -3e38, ALU.add, ALU.max, SMALL[:, 0:1]))
                v.tensor_scalar(SMALL[:, 2 + t % 2:3 + t % 2], SMALL[:, 0:1], -1.0, None, ALU.mult).then_inc(s2_max, 1)

            def output2(t):
                i, h = divmod(t, HEADS)
                base = (t % 2) * 3 * HALF + 2 * HALF + HD
                dve.wait_ge(o2_ready, t + 1)
                if t >= 1:
                    dve.wait_ge(o2_taken, t)
                then(v.reciprocal(SMALL[:, 6:7], SMALL[:, 76 + t % 4:77 + t % 4]))
                v.tensor_scalar(YT2[:, i, h * HD:(h + 1) * HD], PS[:, base:base + HD], SMALL[:, 6:7], None,
                                ALU.mult).then_inc(o2_taken, 1)
                if h == HEADS - 1:
                    dve.wait_ge(o2_taken, t + 1)
                    then(v.tensor_tensor(YSQ[:], YT2[:, i, :], YT2[:, i, :], ALU.mult))
                    v.tensor_reduce(SMALL[:, 8 + 8 * i:16 + 8 * i], YSQ[:].rearrange("p (a b) -> p a b", a=HEADS), AX.X,
                                    ALU.add).then_inc(ysum_ready, 1)
                    dve.wait_ge(ysum_ready, i + 1)

            maxima2(0)
            maxima2(1)
            for t in range(UNITS2):
                if t + 2 < UNITS2 - HEADS:
                    maxima2(t + 2)
                    output2(t)
                else:
                    output2(t)
                    if t + 2 < UNITS2:
                        maxima2(t + 2)
            dve.wait_ge(yroot, 1)
            then(v.reciprocal(SMALL[:, 8:72], SMALL[:, 8:72]))
            for i in range(NB):
                for h in range(HEADS):
                    y = YT2[:, i, h * HD:(h + 1) * HD]
                    ins = v.tensor_scalar(y, y, SMALL[:, 8 + 8 * i + h:9 + 8 * i + h], None, ALU.mult)
                ins.then_inc(ynorm, 1)
            for c in range(4):
                dve.wait_ge(y2_turned, c + 1)
                v.tensor_copy(Q2[:, c, :], slot(c)).then_inc(y2_ready, 1)
            for k in range(KD):
                lo(SP_OUT2, k, Q2[:, k, :] if k < 4 else CU[:, k - 4, META:], G_OUTN)
            for k in range(KD):
                use = USE0 + C_OUT2 + k
                dve.wait_ge(psum_full, use + 1)
                v.tensor_tensor(X[:, k, :], X[:, k, :], slot(use), ALU.add).then_inc(evacuated, 1)
            for k in range(KD):
                lo(SP_MLP, k, X[:, k, :], G_MLP)
            for k in range(KD):
                add_square(N_MLP, k)
            norm(N_MLP)

            def hidden(g, use, i=None):
                n_c, n_u = (0, 0) if i is None else (i * (2 * FG), i * 24)

                def low(j):
                    dve.wait_ge(a_hi, n_c + (FG * g + j + 1))
                    v.tensor_tensor(AL[:, g % 2, j, :], TM[:, j % 2, :], AH[:, g % 2, j, :].bitcast(F32),
                                    ALU.subtract).then_inc(a_split, 1)

                for j in range(FG):
                    if g > 0 or j >= 2:
                        dve.wait_ge(a_split, n_c + (FG * g + j - 1))
                    dve.wait_ge(psum_full, n_u + (use + j + 1))
                    v.scalar_tensor_tensor(out=TM[:, j % 2, :], in0=slot(use + j), scalar=0.0, in1=RB[:], op0=ALU.max,
                                           op1=ALU.mult).then_inc(evacuated, 1)
                    if j >= 1:
                        low(j - 1)
                low(FG - 1)

            def add_out(use, i=None):
                n_u = 0 if i is None else i * 24
                for e in range(KD):
                    dve.wait_ge(psum_full, n_u + (use + e + 1))
                    v.tensor_tensor(X[:, e, :], X[:, e, :], slot(use + e), ALU.add).then_inc(evacuated, 1)

            use = USE_MLP
            hidden(0, use)
            with dve.Fori(0, 3) as i:
                for g in range(2):
                    hidden(g + 1, use + FG + 3 * FG * g, i)
                    add_out(use + 2 * FG + 3 * FG * g, i)
            use = USE_MLP + FG + 18 * FG
            hidden(NG - 1, use)
            add_out(use + FG)
            add_out(use + 3 * FG)
            dve.wait_ge(gfin_in, 16)
            for b in range(NB):
                dve.wait_ge(o_root, b + 1)
                r = SMALL[:, 80:81]
                if b >= 1:
                    dve.wait_ge(o_ready, b)
                then(v.reciprocal(r, SMALL[:, 78 + b % 2:79 + b % 2]))
                if b >= 2:
                    dve.wait_ge(stored[b % 2], 16 * (b // 2))
                v.scalar_tensor_tensor(out=OT[:, b % 2, :], in0=slot(USE_MLP + 3 * NG * FG + b), scalar=r, in1=GFIN[:],
                                       op0=ALU.mult, op1=ALU.mult).then_inc(o_ready, 1)


def _stream(np, w):
    n = w.shape[1] // P
    return w.reshape(KD, P, n, P).transpose(2, 1, 0, 3).reshape(n, P, D)


def _columns(np, v):
    return v.reshape(-1, P).T


def kernel(**inputs):
    import numpy as np
    import concourse.bacc as bacc
    from concourse.bass_utils import run_bass_kernel_spmd

    a = {k: np.asarray(v) for k, v in inputs.items()}
    w = a["a_w_in"][0]
    q = w[:, 0:512].reshape(D, 2, GROUP, HD).transpose(0, 2, 1, 3).reshape(D, 512)
    k, v, ga, u, gb = w[:, 512:640], w[:, 640:768], w[:, 768:1280], w[:, 1280:1792], w[:, 1792:2304]
    parts = [_stream(np, m) for m in (q, k, v, u, gb, ga, a["ab_w_out"][0])]
    w = a["c_w_in"][0].reshape(D, 3, KD, P).transpose(0, 2, 1, 3).reshape(D, 3 * D)
    parts += [_stream(np, w), _stream(np, a["c_w_out"][0])]
    w = a["w_in_2"][0]
    q, k, v, f, b, c, u = (w[:, 0:512], w[:, 512:1024], w[:, 1024:1536], w[:, 1536:1544], w[:, 1544:2056],
                           w[:, 2056:2568], w[:, 2568:3080])
    cu = np.stack([c.reshape(D, 4, P), u.reshape(D, 4, P)], 2).reshape(D, D)
    fp = np.concatenate([f, np.zeros((D, P - HEADS), f.dtype)], 1)
    parts += [_stream(np, m) for m in (cu, b, fp, v, k, q, a["w_out_2"][0])]
    w1 = _stream(np, a["w_ff1_2"][0])
    w2 = a["w_ff2_2"][0].reshape(NG, FG, P, FG, 2, P).transpose(0, 3, 2, 4, 1, 5).reshape(NG, FG, P, D)
    parts.append(w1[0:FG])
    for g in range(NG - 1):
        parts += [w1[(g + 1) * FG:(g + 2) * FG], w2[g]]
    parts.append(w2[NG - 1])
    gains = np.stack([_columns(np, t) for t in (
        a["pre_norm"][0], a["post_norm"][0], a["pre_norm"][1], a["post_norm"][1], a["c_dw_b"][0], a["c_ln_g"][0],
        a["c_ln_b"][0], a["norm_mix_g_2"][0], a["out_norm_g_2"][0], a["norm_mlp_g_2"][0])], 1)
    arrays = {
        "x": a["x"][0],
        "meta": a["meta_tokens_2"],
        "weights": np.concatenate(parts, 0),
        "gains": gains,
        "taps": a["c_dw_w"][0, :, 0, :].reshape(TAPS, KD, P).transpose(2, 1, 0),
        "pool_w": a["b_pool_w"][0].transpose(1, 0, 2),
        "pool_scale": _columns(np, a["b_pool_scale"][0]),
        "conv_w": a["conv_w_2"][0].reshape(3, 4, P).transpose(2, 1, 0),
        "b_f": a["b_f_2"][0].reshape(HEADS, 1),
        "sinks": np.broadcast_to(a["a_sinks"][0], (P, HEADS)),
        "final_g": np.broadcast_to(a["final_norm_g_2"], (P, D)),
    }
    nc = bacc.Bacc("TRN2", target_bir_lowering=False, num_devices=1)
    args = []
    for name, t in arrays.items():
        arrays[name] = t = np.ascontiguousarray(t)
        args.append(nc.dram_tensor(name, t.shape, mybir.dt.from_np(t.dtype), kind="ExternalInput").ap())
    args.append(nc.dram_tensor("out", (S, D), F32, kind="ExternalOutput").ap())
    build(nc, *args)
    r = run_bass_kernel_spmd(nc, [arrays], core_ids=[0])
    return r.results[0]["out"].reshape(1, S, D)
```
